# Optimizing a Trainium2 kernel written in Bass

```python
import math
import jax, jax.numpy as jnp
from jax import lax
import numpy as np

D_MODEL = 1024
BATCH = 1
SEQ = 256
DEPTH = 2

CTX_LEN = 256
GRID_W = 64
EPS = 1e-6

DN_HEADS = 4
DN_HEAD_DIM = 128
DN_WIDTH = DN_HEADS * DN_HEAD_DIM
SHORT_CONV = 4
DN_CHUNK = 64

POOL_WINDOWS = (2, 4, 8, 16)
POOL_GROUPS = 4
POOL_WIDTH = D_MODEL // 2
POOL_GW = POOL_WIDTH // POOL_GROUPS

IN_SIZES = (3 * DN_WIDTH, DN_WIDTH, POOL_WIDTH, 2 * DN_HEADS, 2 * DN_HEADS, D_MODEL, D_MODEL)
IN_COLS = 3 * DN_WIDTH + DN_WIDTH + POOL_WIDTH + 4 * DN_HEADS + 2 * D_MODEL

PEER_HEADS = 8
N_KEYS = 128
N_EXPERTS = N_KEYS * N_KEYS
PEER_TOPK = 16
PEER_QDIM = 256
PEER_HALF = PEER_QDIM // 2
PEER_BLOCK = 128

kernel_name = 'hybrid_deltanet_pool_peer_diffusion'

def rmsnorm(x, w):
    xf = x.astype(jnp.float32)
    y = xf * lax.rsqrt(jnp.mean(xf * xf, axis=-1, keepdims=True) + EPS) * w.astype(jnp.float32)
    return y.astype(x.dtype)

def modulate(h, shift, scale):
    return h * (1 + scale) + shift

def l2norm(x):
    return x * lax.rsqrt(jnp.sum(x * x, axis=-1, keepdims=True) + EPS)

def split_columns(p):
    return jnp.split(p, np.cumsum(IN_SIZES)[:-1].tolist(), axis=-1)

def short_conv_silu(x, w):
    T = x.shape[1]
    left = SHORT_CONV // 2
    xp = jnp.pad(x, ((0, 0), (left, SHORT_CONV - 1 - left), (0, 0)))
    y = xp[:, 0:T, :] * w[0]
    for j in range(1, SHORT_CONV):
        y = y + xp[:, j:j + T, :] * w[j]
    return jax.nn.silu(y)

def dn_inputs(qkv, b_raw, a_raw, conv_w, a_log, dt_bias):
    Bn, T, _ = qkv.shape
    qkv = short_conv_silu(qkv, conv_w).astype(jnp.float32)
    q, k, v = jnp.split(qkv, 3, axis=-1)
    heads = lambda t: t.reshape(Bn, T, DN_HEADS, DN_HEAD_DIM).transpose(0, 2, 1, 3)
    q, k, v = l2norm(heads(q)), l2norm(heads(k)), heads(v)
    dirs = lambda t: t.astype(jnp.float32).reshape(Bn, T, 2, DN_HEADS).transpose(2, 0, 3, 1)
    beta = jax.nn.sigmoid(dirs(b_raw))
    a_f = a_log.astype(jnp.float32)[:, None, :, None]
    dtb = dt_bias.astype(jnp.float32)[:, None, :, None]
    g = -jnp.exp(a_f) * jax.nn.softplus(dirs(a_raw) + dtb)
    return (q, k, v, beta, g)

def gated_delta_rule(q, k, v, beta, g, state):
    Bn, Hn, T, DK = q.shape
    DV = v.shape[-1]
    C = DN_CHUNK
    n = T // C
    q = q * (DK ** -0.5)
    chunks = lambda t: t.reshape((Bn, Hn, n, C) + t.shape[3:])
    qc, kc, vc, bc = chunks(q), chunks(k), chunks(v), chunks(beta)
    gcum = jnp.cumsum(chunks(g), axis=-1)
    incl = jnp.tril(jnp.ones((C, C), bool))
    strict = jnp.tril(jnp.ones((C, C), bool), -1)
    decay = jnp.exp(jnp.where(incl, gcum[..., :, None] - gcum[..., None, :], -jnp.inf))
    kb = kc * bc[..., None]
    lower = jnp.where(strict, jnp.einsum('bhnid,bhnjd->bhnij', kb, kc) * decay, 0.0)
    eye = jnp.eye(C, dtype=jnp.float32)
    tinv = lax.linalg.triangular_solve(eye + lower, jnp.broadcast_to(eye, lower.shape),
                                       left_side=True, lower=True, unit_diagonal=True)
    w = tinv @ (kb * jnp.exp(gcum)[..., None])
    u = tinv @ (vc * bc[..., None])
    qg = qc * jnp.exp(gcum)[..., None]
    intra = jnp.einsum('bhnid,bhnjd->bhnij', qc, kc) * decay
    g_last = gcum[..., -1]
    kdec = kc * jnp.exp(g_last[..., None] - gcum)[..., None]

    def step(S, xs):
        w_i, u_i, qg_i, intra_i, kdec_i, gl_i = xs
        v_new = u_i - w_i @ S
        o_i = qg_i @ S + intra_i @ v_new
        S = S * jnp.exp(gl_i)[..., None, None] + jnp.swapaxes(kdec_i, -1, -2) @ v_new
        return S, o_i

    mv = lambda t: jnp.moveaxis(t, 2, 0)
    S, o = lax.scan(step, state, (mv(w), mv(u), mv(qg), mv(intra), mv(kdec), mv(g_last)))
    o = jnp.moveaxis(o, 0, 2).reshape(Bn, Hn, T, DV)
    return o, S

def bidirectional_delta(lat, ctx):
    ql, kl, vl, bl, gl = lat
    qc, kc, vc, bc, g_c = ctx
    s0 = jnp.zeros(qc.shape[:2] + (DN_HEAD_DIM, DN_HEAD_DIM), jnp.float32)
    rev = lambda t: jnp.flip(t, axis=2)
    oc_f, sc_f = gated_delta_rule(qc, kc, vc, bc[0], g_c[0], s0)
    ol_f, _ = gated_delta_rule(ql, kl, vl, bl[0], gl[0], sc_f)
    oc_b, sc_b = gated_delta_rule(rev(qc), rev(kc), rev(vc), rev(bc[1]), rev(g_c[1]), s0)
    ol_b, _ = gated_delta_rule(rev(ql), rev(kl), rev(vl), rev(bl[1]), rev(gl[1]), sc_b)
    return ol_f + rev(ol_b), oc_f + rev(oc_b)

def dn_output(o, z, onorm):
    Bn, Hn, T, DV = o.shape
    o = jnp.swapaxes(o, 1, 2)
    zf = z.astype(jnp.float32).reshape(Bn, T, Hn, DV)
    y = o * lax.rsqrt(jnp.mean(o * o, axis=-1, keepdims=True) + EPS) * onorm.astype(jnp.float32) * jax.nn.silu(zf)
    return y.reshape(Bn, T, Hn * DV).astype(z.dtype)

def pool_minus_self(x, window):
    L = x.shape[-2]
    xf = x.astype(jnp.float32)
    cs = jnp.cumsum(xf, axis=-2)
    P = jnp.concatenate([jnp.zeros_like(cs[..., :1, :]), cs], axis=-2)
    t = jnp.arange(L)
    lo = jnp.clip(t - window // 2, 0, L)
    hi = jnp.clip(t + window - window // 2, 0, L)
    s = jnp.take(P, hi, axis=-2) - jnp.take(P, lo, axis=-2)
    cnt = (hi - lo).astype(jnp.float32)[:, None]
    return s / cnt - xf

def multiscale_pool(p, pool_w, pool_scale, rows):
    Bn, T, _ = p.shape
    if rows is None:
        pg = p.reshape(Bn, T, POOL_GROUPS, POOL_GW)
    else:
        pg = p.reshape(Bn, rows, GRID_W, POOL_GROUPS, POOL_GW)
    y = jnp.stack([pool_minus_self(pg[..., gi, :], win) for gi, win in enumerate(POOL_WINDOWS)], axis=-2)
    y = y.reshape(Bn, T, POOL_GROUPS, POOL_GW)
    y = jnp.einsum('btgc,gcd->btgd', y, pool_w).reshape(Bn, T, POOL_WIDTH)
    return (y * pool_scale).astype(p.dtype)

def merge_branches(y_dn, y_pool, gate_dn, gate_pool, w_up_dn, w_up_pool, w_out):
    m = jax.nn.sigmoid(gate_dn) * (y_dn @ w_up_dn) + jax.nn.sigmoid(gate_pool) * (y_pool @ w_up_pool)
    return m @ w_out

def peer_ffn(h, wq, keys, u_tab, v_tab):
    Bn, T, D = h.shape
    tok = h.reshape(-1, PEER_BLOCK, D)

    def block(hb):
        q = (hb @ wq).reshape(PEER_BLOCK, PEER_HEADS, 2, PEER_HALF)
        s = jnp.einsum('nhpd,hpkd->nhpk', q, keys)
        s1, i1 = lax.top_k(s[:, :, 0], PEER_TOPK)
        s2, i2 = lax.top_k(s[:, :, 1], PEER_TOPK)
        cand_s = (s1[..., :, None] + s2[..., None, :]).reshape(PEER_BLOCK, PEER_HEADS, PEER_TOPK * PEER_TOPK)
        cand_i = (i1[..., :, None] * N_KEYS + i2[..., None, :]).reshape(PEER_BLOCK, PEER_HEADS, PEER_TOPK * PEER_TOPK)
        top_s, pos = lax.top_k(cand_s, PEER_TOPK)
        e = jnp.take_along_axis(cand_i, pos, axis=-1)
        gsc = jax.nn.softmax(top_s.astype(jnp.float32), axis=-1)
        a = jnp.einsum('nhkd,nd->nhk', u_tab[e], hb)
        act = (gsc * jax.nn.gelu(a.astype(jnp.float32), approximate=False)).astype(hb.dtype)
        return jnp.einsum('nhk,nhkd->nd', act, v_tab[e])

    return lax.map(block, tok).reshape(Bn, T, D)

def hybrid_layer(x, xc, mod, modc, w_in, conv_w, a_log, dt_bias, dn_out_norm, pool_w, pool_scale,
                 w_up_dn, w_up_pool, w_out, norm_mix, norm_ffn, peer_wq, peer_keys, peer_u, peer_v, update_ctx):
    rows = x.shape[1] // GRID_W
    sh1, sc1, gt1, sh2, sc2, gt2 = jnp.split(mod, 6, axis=-1)
    csh1, csc1, cgt1, csh2, csc2, cgt2 = jnp.split(modc, 6, axis=-1)
    qkv, z, pin, b_raw, a_raw, gd, gp = split_columns(modulate(rmsnorm(x, norm_mix), sh1, sc1) @ w_in)
    qkv_c, z_c, pin_c, b_raw_c, a_raw_c, gd_c, gp_c = split_columns(modulate(rmsnorm(xc, norm_mix), csh1, csc1) @ w_in)
    o_lat, o_ctx = bidirectional_delta(dn_inputs(qkv, b_raw, a_raw, conv_w, a_log, dt_bias),
                                       dn_inputs(qkv_c, b_raw_c, a_raw_c, conv_w, a_log, dt_bias))
    y_dn = dn_output(o_lat, z, dn_out_norm)
    y_pool = multiscale_pool(pin, pool_w, pool_scale, rows)
    x = x + gt1 * merge_branches(y_dn, y_pool, gd, gp, w_up_dn, w_up_pool, w_out)
    x = x + gt2 * peer_ffn(modulate(rmsnorm(x, norm_ffn), sh2, sc2), peer_wq, peer_keys, peer_u, peer_v)
    if update_ctx:
        y_dn_c = dn_output(o_ctx, z_c, dn_out_norm)
        y_pool_c = multiscale_pool(pin_c, pool_w, pool_scale, None)
        xc = xc + cgt1 * merge_branches(y_dn_c, y_pool_c, gd_c, gp_c, w_up_dn, w_up_pool, w_out)
        xc = xc + cgt2 * peer_ffn(modulate(rmsnorm(xc, norm_ffn), csh2, csc2), peer_wq, peer_keys, peer_u, peer_v)
    return x, xc

def setup_inputs(seed: int = 0) -> dict:
    key = jax.random.key(seed)
    ks = jax.random.split(key, 24)
    f32 = jnp.float32
    nrm = lambda k, shape, scale: jax.random.normal(k, shape, f32) * scale
    gain = lambda k, shape: 1.0 + 0.02 * jax.random.normal(k, shape, f32)
    dt = jnp.exp(jax.random.uniform(ks[10], (DEPTH, 2, DN_HEADS), f32, math.log(1e-3), math.log(1e-1)))
    return {
        'x': nrm(ks[0], (BATCH, SEQ, D_MODEL), 1.0),
        'c': nrm(ks[1], (BATCH, D_MODEL), 1.0),
        'ctx': nrm(ks[2], (BATCH, CTX_LEN, D_MODEL), 1.0),
        'c_ctx': nrm(ks[3], (D_MODEL,), 1.0),
        'w_mod': nrm(ks[4], (DEPTH, D_MODEL, 6 * D_MODEL), 0.5 * D_MODEL ** -0.5),
        'b_mod': nrm(ks[5], (DEPTH, 6 * D_MODEL), 0.02),
        'norm_mix': gain(ks[6], (DEPTH, D_MODEL)),
        'w_in': nrm(ks[7], (DEPTH, D_MODEL, IN_COLS), D_MODEL ** -0.5),
        'conv_w': nrm(ks[8], (DEPTH, SHORT_CONV, 3 * DN_WIDTH), SHORT_CONV ** -0.5),
        'a_log': jnp.log(jax.random.uniform(ks[9], (DEPTH, 2, DN_HEADS), f32, 1.0, 16.0)),
        'dt_bias': dt + jnp.log(-jnp.expm1(-dt)),
        'dn_out_norm': gain(ks[11], (DEPTH, DN_HEAD_DIM)),
        'pool_w': nrm(ks[12], (DEPTH, POOL_GROUPS, POOL_GW, POOL_GW), POOL_GW ** -0.5),
        'pool_scale': gain(ks[13], (DEPTH, POOL_WIDTH)),
        'w_up_dn': nrm(ks[14], (DEPTH, DN_WIDTH, D_MODEL), DN_WIDTH ** -0.5),
        'w_up_pool': nrm(ks[15], (DEPTH, POOL_WIDTH, D_MODEL), POOL_WIDTH ** -0.5),
        'w_out': nrm(ks[16], (DEPTH, D_MODEL, D_MODEL), D_MODEL ** -0.5),
        'norm_ffn': gain(ks[17], (DEPTH, D_MODEL)),
        'peer_wq': nrm(ks[18], (DEPTH, D_MODEL, PEER_HEADS * PEER_QDIM), D_MODEL ** -0.5),
        'peer_keys': nrm(ks[19], (DEPTH, PEER_HEADS, 2, N_KEYS, PEER_HALF), PEER_HALF ** -0.5),
        'peer_u': nrm(ks[20], (DEPTH, N_EXPERTS, D_MODEL), D_MODEL ** -0.5),
        'peer_v': nrm(ks[21], (DEPTH, N_EXPERTS, D_MODEL), 1.0),
        'final_norm': gain(ks[22], (D_MODEL,)),
    }

def reference(x, c, ctx, c_ctx, w_mod, b_mod, norm_mix, w_in, conv_w, a_log, dt_bias, dn_out_norm,
              pool_w, pool_scale, w_up_dn, w_up_pool, w_out, norm_ffn, peer_wq, peer_keys, peer_u, peer_v,
              final_norm):
    xc = ctx
    for i in range(DEPTH):
        mod = (jax.nn.silu(c) @ w_mod[i] + b_mod[i])[:, None, :].astype(x.dtype)
        modc = (jax.nn.silu(c_ctx) @ w_mod[i] + b_mod[i])[None, None, :].astype(x.dtype)
        x, xc = hybrid_layer(x, xc, mod, modc, w_in[i], conv_w[i], a_log[i], dt_bias[i], dn_out_norm[i],
                             pool_w[i], pool_scale[i], w_up_dn[i], w_up_pool[i], w_out[i], norm_mix[i],
                             norm_ffn[i], peer_wq[i], peer_keys[i], peer_u[i], peer_v[i], i < DEPTH - 1)
    return rmsnorm(x, final_norm)


_drawn_inputs = setup_inputs


def setup_inputs(seed=0):
    import zlib

    import numpy as np

    out = dict(_drawn_inputs(seed))
    spreads = {}
    factors = {'dn_out_norm': 3.172, 'final_norm': 7.954, 'pool_scale': 3.034}
    for name, (base, spread) in spreads.items():
        noise = np.random.default_rng([zlib.crc32(name.encode()), seed]).standard_normal(out[name].shape)
        drawn = base * np.exp(spread * noise) if base else spread * noise
        out[name] = __import__('jax').numpy.asarray(drawn.astype(out[name].dtype))
    for name, factor in factors.items():
        out[name] = (out[name] * factor).astype(out[name].dtype)
    return out
```

```python
from contextlib import ExitStack

import numpy as np

import concourse.bass as bass
from concourse import mybir

F32 = mybir.dt.float32
U32 = mybir.dt.uint32
ALU = mybir.AluOpType
ACT = mybir.ActivationFunctionType
AX = mybir.AxisListType

P = 128
D = 1024
KD = D // P
SEQ = 256
TILES = 4
TOK = TILES * P
DEPTH = 2
EPS = 1e-6
HEADS = 4
DNW = HEADS * P
IN_COLS = 4624
COL_BA, COL_GD, COL_GP = 2560, 2576, 3600
BANK = 512
CONV = 4
GRID_W = 64
POOLW = (2, 4, 8, 16)
PADS = 8
CTXP = SEQ + 2 * PADS
LATP = GRID_W + 2 * PADS
PBUF = CTXP + (SEQ // GRID_W) * LATP
PH = 8
TOPK = 16
NEXP = 16384
LEVELS = 7
BIG = 1e30
FILL = -3e38

ROWN = [TOPK // (i + 1) for i in range(TOPK)]
NC = sum(ROWN)
PAIR = 2 * TOPK
PAIRS = PH // 2
UR, VR = 16, 8
DR = VR

C_ID, C_ONE, C_TRF, C_TRB, C_NEF, C_NEB, C_SEL, C_IOTA = 0, 128, 256, 384, 512, 640, 768, 1024
C_END = C_IOTA + NC
V_GT1, V_SH2, V_A2, V_GT2 = range(4)


def constants():
    m, i = np.arange(P)[:, None], np.arange(P)[None, :]
    c = np.zeros((P, C_END), np.float32)
    c[:, C_ID:C_ID + P] = m == i
    c[:, C_ONE:C_ONE + P] = 1
    c[:, C_TRF:C_TRF + P] = m <= i
    c[:, C_TRB:C_TRB + P] = m >= i
    c[:, C_NEF:C_NEF + P] = np.where(i >= m, 0, -BIG)
    c[:, C_NEB:C_NEB + P] = np.where(i <= m, 0, -BIG)
    c[0, C_SEL:C_SEL + P] = 1
    c[1, C_SEL + P:C_SEL + 2 * P] = 1
    c[:, C_IOTA:C_END] = np.arange(NC)
    lv = np.zeros((P, 2, LEVELS, P), np.float32)
    for n in range(LEVELS):
        s = 1 << n
        same = (m // (2 * s)) == (i // (2 * s))
        lv[:, 0, n] = same & (m % (2 * s) < s) & (i % (2 * s) >= s)
        lv[:, 1, n] = same & (m % (2 * s) >= s) & (i % (2 * s) < s)
    ic = np.zeros((4, TOK), np.float32)
    for g, w in enumerate(POOLW):
        for row, start, length in [(0, 0, SEQ)] + [(r, SEQ + r * GRID_W, GRID_W) for r in range(SEQ // GRID_W)]:
            t = np.arange(length)
            n = np.clip(t + w - w // 2, 0, length) - np.clip(t - w // 2, 0, length)
            ic[g, start:start + length] = 1.0 / n
    ic = np.broadcast_to(ic.reshape(1, 4 * TOK), (P, 4 * TOK))
    return c, np.ascontiguousarray(lv.reshape(P, -1)), np.ascontiguousarray(ic)


class Own:

    def __init__(self, eng, sem):
        self.eng, self.sem, self.n = eng, sem, 0

    def __call__(self, ins):
        ins.then_inc(self.sem, 1)
        self.n += 1
        return self.n

    def wait(self, n=None):
        self.eng.wait_ge(self.sem, self.n if n is None else n)

    def then(self, ins):
        self(ins)
        self.wait()

    def clear(self):
        self.wait()
        self.eng.sem_clear(self.sem)
        self.n = 0


class Keep:
    pass


class Phase:

    def __init__(self, nc, ctx, name):
        self.nc, self.ctx, self.name, self.sems = nc, ctx, name, []
        ctx.callback(self.close)

    def close(self):
        self.nc.clear_and_free_semaphores(self.sems)
        self.nc.all_engine_barrier()

    def sb(self, name, shape, dt=F32):
        return self.ctx.enter_context(self.nc.sbuf_tensor(f"{self.name}_{name}", shape, dt))

    def sem(self, name):
        self.sems.append(self.nc.alloc_semaphore(f"{self.name}_{name}"))
        return self.sems[-1]


def mod_phase(nc, K, W, layer):
    with ExitStack() as ctx:
        ph = Phase(nc, ctx, f"mod{layer}")
        NW, NCH = 4, 6 * D // BANK
        cv = ph.sb("cv", [P, 2, KD])
        sg = ph.sb("sg", [P, 2, KD])
        sT = ph.sb("sT", [P, KD, 2])
        w = ph.sb("w", [P, NW, KD, BANK])
        mod = ph.sb("mod", [2, 6 * D])
        bm = ph.sb("bm", [2, 6 * D])
        nrm = ph.sb("nrm", [2, 2, D])
        small_in, x_in = ph.sem("small_in"), ph.sem("x_in")
        w_in = [ph.sem(f"w_in{i}") for i in range(NW)]
        sig_ready, silu_ready = ph.sem("sig_ready"), ph.sem("silu_ready")
        rows_ready, rows_out = ph.sem("rows_ready"), ph.sem("rows_out")
        gains_ready = ph.sem("gains_ready")
        cols_ready, cols_out, rows_stored = ph.sem("cols_ready"), ph.sem("cols_out"), ph.sem("rows_stored")
        v_own = ph.sem("v_own")
        with nc.Block() as block:
            @block.sync
            def _(sp):
                if layer == 0:
                    sp.dma_start(K.cst[:], W.cst).then_inc(small_in, 16)
                sp.dma_start(cv[:, 0, :], W.c_ctx.rearrange("(p k) -> p k", k=KD)).then_inc(small_in, 16)
                sp.dma_start(cv[:, 1, :], W.c[0].rearrange("(p k) -> p k", k=KD)).then_inc(small_in, 16)
                for s in range(2):
                    sp.dma_start(bm[s:s + 1, :], W.b_mod[layer:layer + 1, :]).then_inc(small_in, 16)
                    sp.dma_start(nrm[s:s + 1, 0, :], W.norm_mix[layer:layer + 1, :]).then_inc(small_in, 16)
                    sp.dma_start(nrm[s:s + 1, 1, :], W.norm_ffn[layer:layer + 1, :]).then_inc(small_in, 16)
                src = W.w_mod[layer].rearrange("(p k) n -> p k n", k=KD)
                for n in range(NCH):
                    if n == NW and layer == 0:
                        for t in range(TILES):
                            tok = W.ctx if t < 2 else W.x
                            sp.dma_start(K.x[:, t, :], tok[0, (t % 2) * P:(t % 2 + 1) * P, :]).then_inc(x_in, 16)
                    if n >= NW:
                        sp.wait_ge(rows_ready, n - NW + 1)
                    sp.dma_start(w[:, n % NW], src[:, :, n * BANK:(n + 1) * BANK]).then_inc(w_in[n % NW], 16)
                sp.wait_ge(gains_ready, 2)
                sp.dma_start(K.rows[layer], mod[:, 2 * D:].rearrange("s (v d) -> s v d", v=4)).then_inc(rows_stored, 16)
                sp.wait_ge(rows_stored, 16)
                if layer == 0:
                    sp.wait_ge(x_in, 16 * TILES)

            small = 16 * (8 + (1 if layer == 0 else 0))

            @block.scalar
            def _(act):
                act.wait_ge(small_in, small)
                act.activation(sg[:], cv[:], ACT.Sigmoid).then_inc(sig_ready, 1)
                act.wait_ge(cols_ready, 1)
                act.activation(K.modT[:], K.bank[0][:, 0:32].rearrange("p (j k s) -> p j k s", j=2, k=KD),
                               ACT.Copy).then_inc(cols_out, 1)

            @block.vector
            def _(dve):
                own = Own(dve, v_own)
                dve.wait_ge(sig_ready, 1)
                dve.tensor_tensor(sT[:].rearrange("p k s -> p s k"), cv[:], sg[:], ALU.mult).then_inc(silu_ready, 1)
                for n in range(NCH):
                    dve.wait_ge(rows_ready, n + 1)
                    cols = slice(n * BANK, (n + 1) * BANK)
                    dve.tensor_tensor(mod[:, cols], K.bank[6 + n % 2][0:2, :], bm[:, cols], ALU.add).then_inc(rows_out, 1)
                dve.wait_ge(rows_out, NCH)
                for j, off in ((0, D), (1, 4 * D)):
                    dve.scalar_tensor_tensor(out=mod[:, off:off + D], in0=mod[:, off:off + D], scalar=1.0,
                                             in1=nrm[:, j, :], op0=ALU.add, op1=ALU.mult).then_inc(gains_ready, 1)

            @block.tensor
            def _(pe):
                pe.wait_ge(silu_ready, 1)
                for n in range(NCH):
                    pe.wait_ge(w_in[n % NW], 16 * (n // NW + 1))
                    if n >= 2:
                        pe.wait_ge(rows_out, n - 1)
                    for k in range(KD):
                        mm = pe.matmul(K.bank[6 + n % 2][0:2, :], sT[:, k, :], w[:, n % NW, k, :],
                                       start=(k == 0), stop=(k == KD - 1))
                    mm.then_inc(rows_ready, 1)
                pe.wait_ge(gains_ready, 2)
                for j, off in ((0, D), (1, 0)):
                    for k in range(KD):
                        c = (j * KD + k) * 2
                        mm = pe.matmul(K.bank[0][:, c:c + 2], mod[0:2, off + k * P:off + (k + 1) * P],
                                       K.cst[0:2, C_ID:C_ID + 2], start=True, stop=True)
                mm.then_inc(cols_ready, 1)


def inproj_phase(nc, K, W, layer):
    with ExitStack() as ctx:
        ph = Phase(nc, ctx, f"inp{layer}")
        NW = 2
        NF = 20
        xn = ph.sb("xn", [P, TILES, D])
        ss = ph.sb("ss", [P, 3, TILES])
        eps = ph.sb("eps", [P, 1])
        w = ph.sb("w", [P, NW, KD, BANK])
        wba = ph.sb("wba", [P, KD, 16])
        cw = ph.sb("cw", [P, CONV, 12])
        raw = ph.sb("raw", [P, 3, 2, SEQ + CONV - 1])
        cv = ph.sb("cv", [P, 2, 2, SEQ])
        sg = ph.sb("sg", [P, 3, TOK])
        pb = ph.sb("pb", [P, 4, PBUF])
        ps = ph.sb("ps", [P, 2, PBUF])
        ic = ph.sb("ic", [P, 4, TOK])
        small_in = ph.sem("small_in")
        w_in = [ph.sem(f"w_in{i}") for i in range(NW)]
        sq_done, rstd_ready, xn_ready = ph.sem("sq_done"), ph.sem("rstd_ready"), ph.sem("xn_ready")
        xT_ready, hT_ready = ph.sem("xT_ready"), ph.sem("hT_ready")
        proj_ready, proj_out = ph.sem("proj_ready"), ph.sem("proj_out")
        ba_ready = ph.sem("ba_ready")
        pads_ready, conv_ready, sig_ready, gated = ph.sem("pads"), ph.sem("conv"), ph.sem("sig"), ph.sem("gated")
        a_own, v_own = ph.sem("a_own"), ph.sem("v_own")
        order = list(range(NF))
        s0 = [1 if layer == 1 and (f < 4 or f >= 12) else 0 for f in range(NF)]
        with nc.Block() as block:
            @block.sync
            def _(sp):
                sp.dma_start(cw[:], W.conv_w[layer]).then_inc(small_in, 16)
                sp.dma_start(ic[:].rearrange("p g t -> p (g t)"), W.icnt).then_inc(small_in, 16)
                sp.dma_start(wba[:], W.w_in[layer].rearrange("(k p) n -> p k n", p=P)[:, :, COL_BA:COL_BA + 16]).then_inc(small_in, 16)
                src = W.w_in[layer].rearrange("(k p) n -> p k n", p=P)
                for n in range(NF // 4):
                    if n >= NW:
                        sp.wait_ge(proj_ready, 4 * (n - NW + 1))
                    sp.dma_start(w[:, n % NW], src[:, :, n * BANK:(n + 1) * BANK]).then_inc(w_in[n % NW], 16)

            @block.gpsimd
            def _(pool):
                pool.memset(eps[:], EPS).then_inc(pads_ready, 1)
                pool.memset(raw[:], 0.0).then_inc(pads_ready, 1)
                pool.memset(pb[:], 0.0).then_inc(pads_ready, 1)

            @block.scalar
            def _(act):
                own = Own(act, a_own)
                act.wait_ge(pads_ready, 3)
                for t in range(TILES):
                    own(act.activation(xn[:, t, :], K.x[:, t, :], ACT.Square, accum_out=ss[:, 0, t:t + 1]))
                own.wait()
                own.then(act.activation(ss[:, 1, :], ss[:, 0, :], ACT.Ln, bias=eps[:], scale=1.0 / D))
                act.activation(ss[:, 2, :], ss[:, 1, :], ACT.Exp, scale=-0.5).then_inc(rstd_ready, 1)
                act.wait_ge(xT_ready, TILES)
                for k in range(KD):
                    for s in range(2):
                        act.activation(K.hT[:, k, s * SEQ:(s + 1) * SEQ], K.bank[k][:, s * SEQ:(s + 1) * SEQ],
                                       ACT.Identity, bias=K.modT[:, 1, k, s:s + 1],
                                       scale=K.modT[:, 0, k, s:s + 1]).then_inc(hT_ready, 1)

                def sigmoid(f):
                    act.wait_ge(conv_ready, f + 1)
                    if f >= 3:
                        act.wait_ge(gated, f - 2)
                    act.activation(sg[:, f % 3, s0[f] * SEQ:], cv[:, f % 2, s0[f]:, :], ACT.Sigmoid).then_inc(sig_ready, 1)

                for f in order:
                    act.wait_ge(proj_ready, f + 1)
                    b = K.bank[f % 8]
                    if f < 12:
                        if f >= 3:
                            act.wait_ge(conv_ready, f - 2)
                        act.activation(raw[:, f % 3, s0[f]:, 2:2 + SEQ],
                                       b[:, s0[f] * SEQ:].rearrange("p (s t) -> p s t", t=SEQ), ACT.Copy).then_inc(proj_out, 1)
                        if f >= 1:
                            sigmoid(f - 1)
                    elif f < 16:
                        if f == 12:
                            sigmoid(11)
                        act.wait_ge(gated, f - 2)
                        act.activation(sg[:, f % 3, s0[f] * SEQ:], b[:, s0[f] * SEQ:], ACT.Sigmoid).then_inc(proj_out, 1)
                    else:
                        g = f - 16
                        if not s0[f]:
                            own(act.activation(pb[:, g, PADS:PADS + SEQ], b[:, 0:SEQ], ACT.Copy))
                            own.wait()
                        act.activation(pb[:, g, CTXP:].rearrange("p (r c) -> p r c", c=LATP)[:, :, PADS:PADS + GRID_W],
                                       b[:, SEQ:].rearrange("p (r c) -> p r c", c=GRID_W), ACT.Copy).then_inc(proj_out, 1)

            @block.vector
            def _(dve):
                own = Own(dve, v_own)
                dve.wait_ge(rstd_ready, 1)
                for t in range(TILES):
                    dve.tensor_scalar(xn[:, t, :], K.x[:, t, :], ss[:, 2, t:t + 1], None, ALU.mult).then_inc(xn_ready, 1)
                dve.wait_ge(small_in, 48)

                def gate(f):
                    dve.wait_ge(sig_ready, f + 1)
                    dve.tensor_tensor(K.qkv[:, f, s0[f] * SEQ:], cv[:, f % 2, s0[f]:, :].rearrange("p s t -> p (s t)"),
                                      sg[:, f % 3, s0[f] * SEQ:], ALU.mult).then_inc(gated, 1)

                for f in order:
                    dve.wait_ge(proj_out, f + 1)
                    if f < 12:
                        out = cv[:, f % 2, s0[f]:, :]
                        if f >= 2:
                            gate(f - 2)
                            dve.wait_ge(gated, f - 1)
                        own.then(dve.tensor_scalar(out, raw[:, f % 3, s0[f]:, 0:SEQ], cw[:, 0, f:f + 1], None, ALU.mult))
                        for j in range(1, CONV):
                            ins = dve.scalar_tensor_tensor(out=out, in0=raw[:, f % 3, s0[f]:, j:j + SEQ], scalar=cw[:, j, f:f + 1],
                                                           in1=out, op0=ALU.mult, op1=ALU.add)
                            if j < CONV - 1:
                                own.then(ins)
                        ins.then_inc(conv_ready, 1)
                        dve.wait_ge(conv_ready, f + 1)
                    elif f < 16:
                        if f == 12:
                            gate(10)
                            gate(11)
                        dve.tensor_tensor(K.zT[:, f - 12, s0[f] * SEQ:], K.bank[f % 8][:, s0[f] * SEQ:],
                                          sg[:, f % 3, s0[f] * SEQ:], ALU.mult).then_inc(gated, 1)
                    else:
                        g = f - 16
                        src, n = pb[:, g, :], PBUF
                        for lv in range(g + 1):
                            step = 1 << lv
                            dst = ps[:, lv % 2, :]
                            own.then(dve.tensor_tensor(dst[:, 0:n - step], src[:, 0:n - step], src[:, step:n], ALU.add))
                            src, n = dst, n - step
                        at = PADS - POOLW[g] // 2
                        parts = []
                        if not s0[f]:
                            parts.append((lambda a, o: a[:, o:o + SEQ], lambda a: a[:, 0:SEQ]))
                        parts.append((lambda a, o: a[:, CTXP:].rearrange("p (r c) -> p r c", c=LATP)[:, :, o:o + GRID_W],
                                      lambda a: a[:, SEQ:].rearrange("p (r c) -> p r c", c=GRID_W)))
                        full = ps[:, g % 2, :]
                        for win, out in parts:
                            own(dve.tensor_tensor(out(K.pT[:, g, :]), win(full, at), out(ic[:, g, :]), ALU.mult))
                        own.wait()
                        for win, out in parts:
                            own(dve.tensor_tensor(out(K.pT[:, g, :]), out(K.pT[:, g, :]), win(pb[:, g, :], PADS), ALU.subtract))
                        own.wait()
                dve.wait_ge(ba_ready, 1)
                dve.tensor_copy(K.ba[:], K.bank[4][:, 0:TILES * 16].rearrange("p (t c) -> p t c", c=16)).then_inc(gated, 1)

            @block.tensor
            def _(pe):
                for t in range(TILES):
                    pe.wait_ge(xn_ready, t + 1)
                    for k in range(KD):
                        mm = pe.transpose(K.bank[k][:, t * P:(t + 1) * P], xn[:, t, k * P:(k + 1) * P], K.cst[:, C_ID:C_ID + P])
                    mm.then_inc(xT_ready, 1)
                pe.wait_ge(hT_ready, 2 * KD)
                for f in order:
                    if f % 4 == 0:
                        pe.wait_ge(w_in[f // 4 % NW], 16 * (f // 4 // NW + 1))
                    if f >= 8:
                        pe.wait_ge(proj_out, f - 7)
                    if 20 > f - 8 >= 12:
                        pe.wait_ge(gated, f - 7)
                    for k in range(KD):
                        mm = pe.matmul(K.bank[f % 8][:, s0[f] * SEQ:], w[:, f // 4 % NW, k, (f % 4) * P:(f % 4 + 1) * P],
                                       K.hT[:, k, s0[f] * SEQ:], start=(k == 0), stop=(k == KD - 1))
                    mm.then_inc(proj_ready, 1)
                pe.wait_ge(small_in, 48)
                pe.wait_ge(gated, 13)
                for t in range(TILES):
                    for k in range(KD):
                        mm = pe.matmul(K.bank[4][:, t * 16:(t + 1) * 16], K.hT[:, k, t * P:(t + 1) * P], wba[:, k, :],
                                       start=(k == 0), stop=(k == KD - 1))
                mm.then_inc(ba_ready, 1)


def delta_phase(nc, K, W, layer):
    with ExitStack() as ctx:
        ph = Phase(nc, ctx, f"dn{layer}")
        OT = [0, 1, 2, 3] if layer == 0 else [2, 3]
        lvl = ph.sb("lvl", [P, 2, LEVELS, P])
        alog = ph.sb("alog", [P, 2, 8])
        onorm = ph.sb("onorm", [P, 1])
        eps = ph.sb("eps", [P, 1])
        sq = ph.sb("sq", [P, 2, TOK])
        rs = ph.sb("rs", [P, 4, TOK])
        nT = K.qkv
        kt = ph.sb("kt", [P, TILES, HEADS, P])
        vt = ph.sb("vt", [P, TILES, HEADS, P])
        gs = ph.sb("gs", [P, 8, TILES, 8])
        tg = ph.sb("tg", [P, 2, HEADS, P])
        em = ph.sb("em", [P, 2, HEADS, P])
        MT = ph.sb("MT", [P, 2, TILES, HEADS, P])
        IT = ph.sb("IT", [P, 2, TILES, HEADS, P])
        ml = ph.sb("ml", [P, 3, HEADS, P])
        wv = ph.sb("wv", [P, 3, HEADS, P])
        T = ph.sb("T", [P, 2, TILES, HEADS, P])
        R = ph.sb("R", [P, 2, TILES, HEADS, P])
        BETA, SPA, SPB, G, CUM, NEGE, DEC, EGL = range(8)
        small_in = ph.sem("small_in")
        eps_ready = ph.sem("eps_ready")
        sq_ready, ssum_ready, rs_ready, n_ready = (ph.sem(n) for n in ("sq_ready", "ssum_ready", "rs_ready", "n_ready"))
        tok_ready, tok_out = ph.sem("tok_ready"), ph.sem("tok_out")
        gate_act, gate_dve, cum_ready, dec_ready = (ph.sem(n) for n in ("gate_act", "gate_dve", "cum_ready", "dec_ready"))
        gram_ready, tg_ready, row_ready, mask_ready, e_ready, mi_ready = (
            ph.sem(n) for n in ("gram_ready", "tg_ready", "row_ready", "mask_ready", "e_ready", "mi_ready"))
        ml_ready, w_ready, w_out, x_ready = (ph.sem(n) for n in ("ml_ready", "w_ready", "w_out", "x_ready"))
        r_ready, tr_ready, t_ready = (ph.sem(n) for n in ("r_ready", "tr_ready", "t_ready"))
        a_own, v_own = ph.sem("a_own"), ph.sem("v_own")
        q0 = [SEQ if layer == 1 and f < 4 else 0 for f in range(8)]
        groups = [(d, t) for t in range(TILES) for d in range(2)]
        NG = len(groups)
        bank = K.bank
        hp = lambda a: a.rearrange("p (h t) -> p h t", t=P)
        ident4 = K.cst[:, C_ID:C_ID + P].unsqueeze(1).broadcast_to([P, HEADS, P])
        with nc.Block() as block:
            @block.sync
            def _(sp):
                sp.dma_start(alog[:, 0, :], W.a_log[layer].rearrange("d h -> (d h)").partition_broadcast(P)).then_inc(small_in, 16)
                sp.dma_start(alog[:, 1, :], W.dt_bias[layer].rearrange("d h -> (d h)").partition_broadcast(P)).then_inc(small_in, 16)
                sp.dma_start(onorm[:], W.dn_out_norm[layer].rearrange("(p o) -> p o", o=1)).then_inc(small_in, 16)
                sp.dma_start(lvl[:].rearrange("p d n t -> p (d n t)"), W.levels).then_inc(small_in, 16)

            @block.gpsimd
            def _(pool):
                pool.memset(eps[:], EPS).then_inc(eps_ready, 1)
                for n in range(1, LEVELS):
                    for g, (d, t) in enumerate(groups):
                        m = (n - 1) * NG + g
                        if m == 0:
                            pool.wait_ge(small_in, 64)
                            pool.wait_ge(mi_ready, NG)
                        if m >= 3:
                            pool.wait_ge(w_ready, m - 2)
                        pool.tensor_tensor(ml[:, m % 3], MT[:, d, t],
                                           lvl[:, d, n].unsqueeze(1).broadcast_to([P, HEADS, P]), ALU.mult).then_inc(ml_ready, 1)

            @block.scalar
            def _(act):
                own = Own(act, a_own)
                act.wait_ge(small_in, 64)
                act.wait_ge(eps_ready, 1)
                for f0 in (0, 4):
                    for f in range(f0, f0 + 4):
                        act.wait_ge(ssum_ready, f + 1)
                        if f >= 4:
                            act.wait_ge(n_ready, f - 3)
                        own(act.activation(rs[:, f % 4, q0[f]:], bank[f % 4][:, q0[f]:], ACT.Ln, bias=eps[:]))
                    own.wait()
                    for f in range(f0, f0 + 4):
                        act.activation(rs[:, f % 4, q0[f]:], rs[:, f % 4, q0[f]:], ACT.Exp, scale=-0.5).then_inc(rs_ready, 1)
                own(act.activation(alog[:, 0, :], alog[:, 0, :], ACT.Exp))
                act.wait_ge(gate_dve, 1)
                own.then(act.activation(gs[:, SPB], gs[:, SPB], ACT.Exp, scale=-1.0))
                act.activation(gs[:, SPB], gs[:, SPB], ACT.Ln, bias=1.0).then_inc(gate_act, 1)
                act.activation(gs[:, BETA], K.ba[:, :, 0:8], ACT.Sigmoid).then_inc(gate_act, 1)
                for n in range(8):
                    act.wait_ge(tok_ready, n + 1)
                    dst = (kt if n < 4 else vt)[:, :, n % 4, :]
                    act.activation(dst, hp(bank[4 + n % 4][:]), ACT.Copy).then_inc(tok_out, 1)
                act.wait_ge(cum_ready, 2)
                own(act.activation(gs[:, NEGE], gs[:, CUM], ACT.Exp))
                own(act.activation(gs[:, DEC], gs[:, DEC], ACT.Exp))
                own(act.activation(gs[:, EGL], gs[:, EGL], ACT.Exp))
                own.wait()
                act.sem_inc(dec_ready, 1)
                for g, (d, t) in enumerate(groups):
                    act.wait_ge(mask_ready, g + 1)
                    for h in range(HEADS):
                        own(act.activation(em[:, g % 2, h], em[:, g % 2, h], ACT.Exp, bias=gs[:, SPA, t, d * 4 + h:d * 4 + h + 1]))
                    own.wait()
                    act.sem_inc(e_ready, 1)
                def turned(m):
                    d, t = groups[m % NG]
                    act.wait_ge(tr_ready, m + 1)
                    act.activation(T[:, d, t], hp(bank[2 + m % 2][:]), ACT.Copy).then_inc(t_ready, 1)

                for m in range(2):
                    turned(m)
                for m in range((LEVELS - 1) * NG):
                    act.wait_ge(w_ready, m + 1)
                    if m >= 3:
                        act.wait_ge(x_ready, m - 2)
                    act.activation(wv[:, m % 3], hp(bank[m % 2][:]), ACT.Copy).then_inc(w_out, 1)
                    if m + 2 < (LEVELS - 1) * NG:
                        turned(m + 2)

            @block.vector
            def _(dve):
                own = Own(dve, v_own)

                def norm(f):
                    dve.wait_ge(rs_ready, f + 1)
                    dve.scalar_tensor_tensor(out=nT[:, f, q0[f]:], in0=K.qkv[:, f, q0[f]:], scalar=(float(P) ** -0.5 if f < 4 else 1.0),
                                             in1=rs[:, f % 4, q0[f]:], op0=ALU.mult, op1=ALU.mult).then_inc(n_ready, 1)

                for f in range(8):
                    if f >= 2:
                        dve.wait_ge(ssum_ready, f - 1)
                    dve.tensor_tensor(sq[:, f % 2, q0[f]:], K.qkv[:, f, q0[f]:], K.qkv[:, f, q0[f]:], ALU.mult).then_inc(sq_ready, 1)
                    if f == 5:
                        for j in range(4):
                            norm(j)
                for j in range(4, 8):
                    norm(j)
                dve.wait_ge(small_in, 64)
                own.then(dve.tensor_tensor(gs[:, SPA], K.ba[:, :, 8:16], alog[:, 1, :].unsqueeze(1).broadcast_to([P, TILES, 8]), ALU.add))
                dve.scalar_tensor_tensor(out=gs[:, SPB], in0=gs[:, SPA], scalar=-1.0, in1=gs[:, SPA], op0=ALU.mult, op1=ALU.max).then_inc(gate_dve, 1)
                dve.wait_ge(gate_act, 2)
                own.then(dve.scalar_tensor_tensor(out=gs[:, SPB], in0=gs[:, SPA], scalar=0.0, in1=gs[:, SPB], op0=ALU.max, op1=ALU.add))
                dve.scalar_tensor_tensor(out=gs[:, G], in0=gs[:, SPB], scalar=-1.0,
                                         in1=alog[:, 0, :].unsqueeze(1).broadcast_to([P, TILES, 8]), op0=ALU.mult, op1=ALU.mult).then_inc(gate_dve, 1)
                dve.wait_ge(cum_ready, 1)
                q = lambda j: bank[3][:, j * 32:(j + 1) * 32].rearrange("p (t c) -> p t c", c=8)
                own(dve.tensor_copy(gs[:, CUM, :, 0:4], q(0)[:, :, 0:4]))
                own(dve.tensor_copy(gs[:, CUM, :, 4:8], q(1)[:, :, 4:8]))
                own(dve.tensor_copy(gs[:, EGL], q(2)))
                own.wait()
                own(dve.tensor_tensor(gs[:, DEC], gs[:, EGL], gs[:, CUM], ALU.subtract))
                own(dve.tensor_scalar(gs[:, SPA], gs[:, CUM], -1.0, None, ALU.mult))
                own.wait()
                dve.sem_inc(cum_ready, 1)
                dve.wait_ge(dec_ready, 1)
                own(dve.tensor_scalar(gs[:, NEGE], gs[:, NEGE], -1.0, None, ALU.mult))
                dve.wait_ge(n_ready, 8)

                def tri(g):
                    d, t = groups[g]
                    if g >= 2:
                        dve.wait_ge(row_ready, g - 1)
                    c = (C_TRF, C_TRB)[d]
                    dve.tensor_tensor(tg[:, g % 2], K.cst[:, c:c + P].unsqueeze(1).broadcast_to([P, HEADS, P]),
                                      gs[:, G, t, d * 4:d * 4 + 4].unsqueeze(2).broadcast_to([P, HEADS, P]), ALU.mult).then_inc(tg_ready, 1)

                tri(0)
                for g, (d, t) in enumerate(groups):
                    if g + 1 < NG:
                        tri(g + 1)
                    dve.wait_ge(row_ready, g + 1)
                    if g >= 2:
                        dve.wait_ge(mi_ready, g - 1)
                    c = (C_NEF, C_NEB)[d]
                    dve.tensor_tensor(em[:, g % 2], hp(bank[6 + g % 2][:]), K.cst[:, c:c + P].unsqueeze(1).broadcast_to([P, HEADS, P]),
                                      ALU.add).then_inc(mask_ready, 1)
                    dve.wait_ge(e_ready, g + 1)
                    dve.wait_ge(gram_ready, t + 1)
                    kk, qk = hp(bank[2 * (t % 2)][:]), hp(bank[2 * (t % 2) + 1][:])
                    if t in OT:
                        own(dve.tensor_tensor(IT[:, d, t], qk, em[:, g % 2], ALU.mult))
                    for h in range(HEADS):
                        own(dve.scalar_tensor_tensor(out=MT[:, d, t, h], in0=kk[:, h], scalar=gs[:, BETA, t, d * 4 + h:d * 4 + h + 1],
                                                     in1=em[:, g % 2, h], op0=ALU.mult, op1=ALU.mult))
                    own.wait()
                    own.then(dve.tensor_tensor(T[:, d, t], MT[:, d, t], lvl[:, d, 0].unsqueeze(1).broadcast_to([P, HEADS, P]), ALU.mult))
                    dve.tensor_tensor(R[:, d, t], ident4, T[:, d, t], ALU.subtract).then_inc(mi_ready, 1)
                for n in range(1, LEVELS):
                    for g, (d, t) in enumerate(groups):
                        m = (n - 1) * NG + g
                        dve.wait_ge(x_ready, m + 1)
                        dve.tensor_tensor(R[:, d, t], R[:, d, t], hp(bank[4 + m % 2][:]), ALU.subtract).then_inc(r_ready, 1)

            @block.tensor
            def _(pe):
                ident = K.cst[:, C_ID:C_ID + P]
                for f in range(8):
                    pe.wait_ge(sq_ready, f + 1)
                    if f >= 4:
                        pe.wait_ge(rs_ready, f - 3)
                    pe.matmul(bank[f % 4][:, q0[f]:], K.cst[:, C_ONE:C_ONE + P], sq[:, f % 2, q0[f]:], start=True, stop=True).then_inc(ssum_ready, 1)
                for n in range(8):
                    src = nT[:, 4 + n, :] if n < 4 else K.qkv[:, 4 + n, :]
                    if n < 4:
                        pe.wait_ge(n_ready, 5 + n)
                    if n >= 4:
                        pe.wait_ge(tok_out, n - 3)
                    for t in range(TILES):
                        mm = pe.transpose(bank[4 + n % 4][:, t * P:(t + 1) * P], src[:, t * P:(t + 1) * P], ident)
                    mm.then_inc(tok_ready, 1)
                pe.wait_ge(gate_dve, 2)
                pe.wait_ge(rs_ready, 8)
                gcols = gs[:, G].rearrange("p t c -> p (t c)")
                for j, c in enumerate((C_TRF, C_TRB, C_ONE)):
                    mm = pe.matmul(bank[3][:, j * 32:(j + 1) * 32], K.cst[:, c:c + P], gcols, start=True, stop=True)
                mm.then_inc(cum_ready, 1)

                def gram(t):
                    if t >= 2:
                        pe.wait_ge(mi_ready, 2 * (t - 1))
                    b = 2 * (t % 2)
                    for h in range(HEADS):
                        k = nT[:, 4 + h, t * P:(t + 1) * P]
                        mm = pe.matmul(bank[b][:, h * P:(h + 1) * P], k, k, start=True, stop=True)
                        if t in OT:
                            mm = pe.matmul(bank[b + 1][:, h * P:(h + 1) * P], k, nT[:, h, t * P:(t + 1) * P], start=True, stop=True)
                    mm.then_inc(gram_ready, 1)

                pe.wait_ge(tok_out, 8)
                pe.wait_ge(cum_ready, 2)
                for g, (d, t) in enumerate(groups):
                    if d == 0:
                        gram(t)
                    pe.wait_ge(tg_ready, g + 1)
                    if g >= 2:
                        pe.wait_ge(mask_ready, g - 1)
                    pe.matmul(bank[6 + g % 2][:], K.cst[:, C_ONE:C_ONE + P], tg[:, g % 2].rearrange("p h t -> p (h t)"),
                              start=True, stop=True).then_inc(row_ready, 1)
                pe.wait_ge(mi_ready, NG)
                last = (LEVELS - 1) * NG

                def turn(m):
                    d, t = groups[m % NG]
                    if m >= NG:
                        pe.wait_ge(r_ready, m - NG + 1)
                    if m >= 2:
                        pe.wait_ge(t_ready, m - 1)
                    for h in range(HEADS):
                        mm = pe.transpose(bank[2 + m % 2][:, h * P:(h + 1) * P], R[:, d, t, h], ident)
                    mm.then_inc(tr_ready, 1)

                def first(m):
                    d, t = groups[m % NG]
                    pe.wait_ge(ml_ready, m + 1)
                    pe.wait_ge(t_ready, m + 1)
                    if m >= 2:
                        pe.wait_ge(w_out, m - 1)
                    for h in range(HEADS):
                        mm = pe.matmul(bank[m % 2][:, h * P:(h + 1) * P], ml[:, m % 3, h], T[:, d, t, h], start=True, stop=True)
                    mm.then_inc(w_ready, 1)

                def second(m):
                    d, t = groups[m % NG]
                    pe.wait_ge(w_out, m + 1)
                    if m >= 2:
                        pe.wait_ge(r_ready, m - 1)
                    for h in range(HEADS):
                        mm = pe.matmul(bank[4 + m % 2][:, h * P:(h + 1) * P], wv[:, m % 3, h], R[:, d, t, h], start=True, stop=True)
                    mm.then_inc(x_ready, 1)

                turn(0)
                turn(1)
                first(0)
                for m in range(last):
                    if m + 1 < last:
                        if m + 2 < last:
                            turn(m + 2)
                        first(m + 1)
                    second(m)

        S, Y = MT[:, 0, 0:2], MT[:, 0, 2:4]
        vn, vd = MT[:, 1, 0:2], MT[:, 1, 2:4]
        qs, os_ = ml[:, 0:2], wv[:, 0:2]
        o, od = T[:, 0], T[:, 1]
        ks_ready, y_ready, z_ready, vn_ready, vd_ready, su_ready, s_ready, iv_ready, qs_out, od_ready = (
            ph.sem(n) for n in ("ks_ready", "y_ready", "z_ready", "vn_ready", "vd_ready", "su_ready", "s_ready", "iv_ready", "qs_out", "od_ready"))
        o2_ready, orstd_ready, on_ready, oT_ready, yT_ready = (ph.sem(n) for n in ("o2_ready", "orstd_ready", "on_ready", "oT_ready", "yT_ready"))
        a2_own, v2_own = ph.sem("a2_own"), ph.sem("v2_own")
        ss = ph.sb("ss", [P, TILES, 3, HEADS])
        scan = [(d, (i, (1, 0, 3, 2)[i])[d]) for i in range(4) for d in range(2)]
        outs = [m for m, (d, t) in enumerate(scan) if t in OT]
        with nc.Block() as block:
            @block.tensor
            def _(pe):
                def ks(m):
                    d, t = scan[m]
                    pe.wait_ge(s_ready, m + 1)
                    B = 4 * d
                    for h in range(HEADS):
                        mm = pe.matmul(bank[B][:, h * P:(h + 1) * P], nT[:, 4 + h, t * P:(t + 1) * P], S[:, d, h], start=True, stop=True)
                    mm.then_inc(ks_ready, 1)
                    if m in outs:
                        if outs.index(m) >= 2:
                            pe.wait_ge(qs_out, outs.index(m) - 1)
                        for h in range(HEADS):
                            mm = pe.matmul(bank[B + 2][:, h * P:(h + 1) * P], nT[:, h, t * P:(t + 1) * P], S[:, d, h], start=True, stop=True)
                        mm.then_inc(iv_ready, 1)

                def z(m):
                    d, t = scan[m]
                    pe.wait_ge(y_ready, m + 1)
                    for h in range(HEADS):
                        mm = pe.matmul(bank[4 * d + 1][:, h * P:(h + 1) * P], R[:, d, t, h], Y[:, d, h], start=True, stop=True)
                    mm.then_inc(z_ready, 1)

                def tail(m):
                    d, t = scan[m]
                    pe.wait_ge(vd_ready, m + 1)
                    for h in range(HEADS):
                        mm = pe.matmul(bank[4 * d][:, h * P:(h + 1) * P], kt[:, t, h], vd[:, d, h], start=True, stop=True)
                    mm.then_inc(su_ready, 1)
                    if m in outs:
                        if outs.index(m) >= 2:
                            pe.wait_ge(od_ready, outs.index(m) - 1)
                        for h in range(HEADS):
                            mm = pe.matmul(bank[4 * d + 3][:, h * P:(h + 1) * P], IT[:, d, t, h], vn[:, d, h], start=True, stop=True)
                        mm.then_inc(iv_ready, 1)

                for m in range(0, len(scan), 2):
                    ks(m)
                    ks(m + 1)
                    z(m)
                    z(m + 1)
                    tail(m)
                    tail(m + 1)
                for n, t in enumerate(OT):
                    pe.wait_ge(on_ready, n + 1)
                    if n >= 2:
                        pe.wait_ge(yT_ready, n - 1)
                    for h in range(HEADS):
                        mm = pe.transpose(bank[n % 2][:, h * P:(h + 1) * P], o[:, t, h], K.cst[:, C_ID:C_ID + P])
                    mm.then_inc(oT_ready, 1)

            @block.scalar
            def _(act):
                own = Own(act, a2_own)
                for n, m in enumerate(outs):
                    d, t = scan[m]
                    act.wait_ge(iv_ready, 4 * (n // 2) + 1 + d)
                    if n >= 2:
                        act.wait_ge(od_ready, n - 1)
                    for h in range(HEADS):
                        own(act.activation(qs[:, d, h], hp(bank[4 * d + 2][:])[:, h], ACT.Copy, scale=gs[:, NEGE, t, d * 4 + h:d * 4 + h + 1]))
                    own.wait()
                    act.sem_inc(qs_out, 1)
                for n, t in enumerate(OT):
                    act.wait_ge(o2_ready, n + 1)
                    own.then(act.activation(ss[:, t, 1], ss[:, t, 0], ACT.Ln, bias=eps[:], scale=1.0 / P))
                    act.activation(ss[:, t, 2], ss[:, t, 1], ACT.Exp, scale=-0.5).then_inc(orstd_ready, 1)

            @block.vector
            def _(dve):
                own = Own(dve, v2_own)
                own.then(dve.memset(S, 0.0))
                dve.sem_inc(s_ready, 2)
                per = lambda j, d, t: gs[:, j, t, d * 4:d * 4 + 4].unsqueeze(2).broadcast_to([P, HEADS, P])

                def y(m):
                    d, t = scan[m]
                    dve.wait_ge(ks_ready, m + 1)
                    for h in range(HEADS):
                        ins = dve.scalar_tensor_tensor(out=Y[:, d, h], in0=hp(bank[4 * d][:])[:, h], scalar=gs[:, NEGE, t, d * 4 + h:d * 4 + h + 1],
                                                       in1=vt[:, t, h], op0=ALU.mult, op1=ALU.add)
                        own(ins)
                    own.wait()
                    dve.sem_inc(y_ready, 1)

                def v(m):
                    d, t = scan[m]
                    dve.wait_ge(z_ready, m + 1)
                    own.then(dve.tensor_tensor(vn[:, d], hp(bank[4 * d + 1][:]), per(BETA, d, t), ALU.mult))
                    dve.tensor_tensor(vd[:, d], vn[:, d], per(DEC, d, t), ALU.mult).then_inc(vd_ready, 1)

                def s(m):
                    d, t = scan[m]
                    dve.wait_ge(su_ready, m + 1)
                    for h in range(HEADS):
                        own(dve.scalar_tensor_tensor(out=S[:, d, h], in0=S[:, d, h], scalar=gs[:, EGL, t, d * 4 + h:d * 4 + h + 1],
                                                     in1=hp(bank[4 * d][:])[:, h], op0=ALU.mult, op1=ALU.add))
                    own.wait()
                    dve.sem_inc(s_ready, 1)

                seen = set()

                def add(m):
                    d, t = scan[m]
                    n = outs.index(m)
                    dve.wait_ge(iv_ready, 4 * (n // 2) + 3 + d)
                    dve.wait_ge(qs_out, n + 1)
                    if t not in seen:
                        own(dve.tensor_tensor(o[:, t], hp(bank[4 * d + 3][:]), qs[:, d], ALU.subtract))
                        seen.add(t)
                    else:
                        own.then(dve.tensor_tensor(os_[:, d], hp(bank[4 * d + 3][:]), qs[:, d], ALU.subtract))
                        own(dve.tensor_tensor(o[:, t], o[:, t], os_[:, d], ALU.add))
                    own.wait()
                    dve.sem_inc(od_ready, 1)

                for m in range(0, len(scan), 2):
                    y(m)
                    y(m + 1)
                    v(m)
                    v(m + 1)
                    s(m)
                    s(m + 1)
                    if m in outs:
                        add(m)
                        add(m + 1)
                for n, t in enumerate(OT):
                    own.then(dve.tensor_tensor(od[:, t], o[:, t], o[:, t], ALU.mult))
                    dve.tensor_reduce(ss[:, t, 0], od[:, t], AX.X, ALU.add).then_inc(o2_ready, 1)
                for n, t in enumerate(OT):
                    dve.wait_ge(orstd_ready, n + 1)
                    dve.tensor_tensor(o[:, t], o[:, t], ss[:, t, 2].unsqueeze(2).broadcast_to([P, HEADS, P]), ALU.mult).then_inc(on_ready, 1)
                for n, t in enumerate(OT):
                    dve.wait_ge(oT_ready, n + 1)
                    dve.scalar_tensor_tensor(out=K.zT[:, :, t * P:(t + 1) * P], in0=hp(bank[n % 2][:]), scalar=onorm[:, 0:1],
                                             in1=K.zT[:, :, t * P:(t + 1) * P], op0=ALU.mult, op1=ALU.mult).then_inc(yT_ready, 1)


def merge_phase(nc, K, W, layer):
    with ExitStack() as ctx:
        ph = Phase(nc, ctx, f"mrg{layer}")
        c0 = 0 if layer == 0 else SEQ
        OT = list(range(c0 // P, TILES))
        gw = ph.sb("gw", [P, 4, KD, BANK])
        up = ph.sb("up", [P, 2, 4, D])
        wo = gw[:, 0:2].rearrange("p j k n -> p (j k n)").rearrange("p (k n) -> p k n", n=D)
        pw = ph.sb("pw", [P, 4, P])
        psc = ph.sb("psc", [P, 4])
        yp = ph.sb("yp", [P, 4, TOK])
        sg = ph.sb("sg", [P, 4, TOK])
        mT = ph.sb("mT", [P, KD, TOK])
        tmp = ph.sb("tmp", [P, 2, BANK])
        gt1 = ph.sb("gt1", [P, 2, D])
        small_in, wo_in = ph.sem("small_in"), ph.sem("wo_in")
        up_in, gt1_in = ph.sem("up_in"), ph.sem("gt1_in")
        g_in = [ph.sem(f"g_in{i}") for i in range(4)]
        lin_ready, lin_out, gate_ready, gate_out = (ph.sem(n) for n in ("lin_ready", "lin_out", "gate_ready", "gate_out"))
        up_ready, up_out, m_ready, y_ready, y_out = (ph.sem(n) for n in ("up_ready", "up_out", "m_ready", "y_ready", "y_out"))
        v_own = ph.sem("v_own")
        bank = K.bank
        with nc.Block() as block:
            @block.sync
            def _(sp):
                sp.dma_start(pw[:], W.pool_w[layer].rearrange("g c d -> c g d")).then_inc(small_in, 16)
                sp.dma_start(psc[:], W.pool_scale[layer]).then_inc(small_in, 16)
                src = W.w_in[layer].rearrange("(k p) n -> p k n", p=P)
                for half in range(2):
                    for j, c in enumerate((COL_GD, COL_GP)):
                        sp.dma_start(gw[:, 2 * half + j], src[:, :, c + half * BANK:c + (half + 1) * BANK]).then_inc(g_in[2 * half + j], 16)
                    if half == 0:
                        sp.dma_start(up[:, 0], W.w_up_dn[layer].rearrange("(k p) n -> p k n", p=P)).then_inc(up_in, 16)
                        sp.dma_start(up[:, 1], W.w_up_pool[layer].rearrange("(k p) n -> p k n", p=P)).then_inc(up_in, 16)
                sp.wait_ge(gate_ready, KD)
                sp.dma_start(wo, W.w_out[layer].rearrange("(k p) n -> p k n", p=P)).then_inc(wo_in, 16)
                for s in range(2):
                    sp.dma_start(gt1[:, s, :], K.rows[layer, s, V_GT1].partition_broadcast(P)).then_inc(gt1_in, 16)

            @block.tensor
            def _(pe):
                pe.wait_ge(small_in, 32)
                for g in range(4):
                    pe.matmul(bank[g][:, c0:], pw[:, g, :], K.pT[:, g, c0:], start=True, stop=True).then_inc(lin_ready, 1)
                for f in range(KD):
                    half, c = f // 4, (f % 4) * P
                    for j in range(2):
                        pe.wait_ge(g_in[2 * half + j], 16)
                        if f == 0:
                            pe.wait_ge(lin_out, 4)
                        if f >= 2:
                            pe.wait_ge(gate_out, 2 * (f - 2) + j + 1)
                        for k in range(KD):
                            mm = pe.matmul(bank[2 * (f % 2) + j][:, c0:], gw[:, 2 * half + j, k, c:c + P], K.hT[:, k, c0:],
                                           start=(k == 0), stop=(k == KD - 1))
                        mm.then_inc(gate_ready, 1)
                    if f == 0:
                        pe.wait_ge(up_in, 32)
                    for j, y in enumerate((K.zT, yp)):
                        if f >= 2:
                            pe.wait_ge(up_out, f - 1)
                        for k in range(4):
                            mm = pe.matmul(bank[4 + 2 * (f % 2) + j][:, c0:], up[:, j, k, f * P:(f + 1) * P], y[:, k, c0:],
                                           start=(k == 0), stop=(k == 3))
                    mm.then_inc(up_ready, 1)
                pe.wait_ge(wo_in, 16)
                pe.wait_ge(gate_out, 2 * KD)
                pe.wait_ge(m_ready, KD)
                for n, (t, half) in enumerate((t, half) for t in OT for half in range(2)):
                    if n >= 4:
                        pe.wait_ge(y_out, n - 3)
                    for k in range(KD):
                        mm = pe.matmul(bank[n % 4][:], mT[:, k, t * P:(t + 1) * P], wo[:, k, half * BANK:(half + 1) * BANK],
                                       start=(k == 0), stop=(k == KD - 1))
                    mm.then_inc(y_ready, 1)

            @block.scalar
            def _(act):
                act.wait_ge(small_in, 32)
                for g in range(4):
                    act.wait_ge(lin_ready, g + 1)
                    act.activation(yp[:, g, c0:], bank[g][:, c0:], ACT.Copy, scale=psc[:, g:g + 1]).then_inc(lin_out, 1)
                for f in range(KD):
                    for j in range(2):
                        act.wait_ge(gate_ready, 2 * f + j + 1)
                        if f >= 2:
                            act.wait_ge(m_ready, f - 1)
                        act.activation(sg[:, 2 * (f % 2) + j, c0:], bank[2 * (f % 2) + j][:, c0:], ACT.Sigmoid).then_inc(gate_out, 1)

            @block.vector
            def _(dve):
                own = Own(dve, v_own)
                for f in range(KD):
                    dve.wait_ge(gate_out, 2 * f + 2)
                    dve.wait_ge(up_ready, f + 1)
                    b = 2 * (f % 2)
                    own(dve.tensor_tensor(sg[:, b, c0:], sg[:, b, c0:], bank[4 + b][:, c0:], ALU.mult))
                    dve.tensor_tensor(sg[:, b + 1, c0:], sg[:, b + 1, c0:], bank[5 + b][:, c0:], ALU.mult).then_inc(up_out, 1)
                    own.wait()
                    dve.wait_ge(up_out, f + 1)
                    dve.tensor_tensor(mT[:, f, c0:], sg[:, b, c0:], sg[:, b + 1, c0:], ALU.add).then_inc(m_ready, 1)
                dve.wait_ge(gt1_in, 32)
                for n, (t, half) in enumerate((t, half) for t in OT for half in range(2)):
                    cols = slice(half * BANK, (half + 1) * BANK)
                    dve.wait_ge(y_ready, n + 1)
                    dve.tensor_tensor(tmp[:, n % 2], bank[n % 4][:], gt1[:, t // 2, cols], ALU.mult).then_inc(y_out, 1)
                    dve.wait_ge(y_out, n + 1)
                    own(dve.tensor_tensor(K.x[:, t, cols], K.x[:, t, cols], tmp[:, n % 2], ALU.add))
                    own.wait()


def query_phase(nc, K, W, layer):
    with ExitStack() as ctx:
        ph = Phase(nc, ctx, f"qry{layer}")
        t0 = 0 if layer == 0 else 2
        c0 = t0 * P
        OT = list(range(t0, TILES))
        NT = len(OT)
        junk = ph.sb("junk", [P, D])
        ss = ph.sb("ss", [P, 3, TILES])
        eps = ph.sb("eps", [P, 1])
        h2T = ph.sb("h2T", [P, KD, TOK])
        wq = ph.sb("wq", [P, 2, KD, BANK])
        a2 = ph.sb("a2", [P, 2, D])
        sh2 = ph.sb("sh2", [P, 2, D])
        qT = ph.sb("qT", [P, 16, TOK])
        kT = ph.sb("kT", [P, 16, P])
        small_in = ph.sem("small_in")
        mod_in = ph.sem("mod_in")
        wq_in = [ph.sem(f"wq_in{i}") for i in range(2)]
        eps_ready, rstd_ready, h2_ready, h2T_ready, h2T_out = (ph.sem(n) for n in ("eps_ready", "rstd_ready", "h2_ready", "h2T_ready", "h2T_out"))
        q_ready, q_out, s_ready, s_out = (ph.sem(n) for n in ("q_ready", "q_out", "s_ready", "s_out"))
        a_own, v_own = ph.sem("a_own"), ph.sem("v_own")
        bank = K.bank
        with nc.Block() as block:
            @block.sync
            def _(sp):
                for s in range(2):
                    sp.dma_start(a2[:, s, :], K.rows[layer, s, V_A2].partition_broadcast(P)).then_inc(mod_in, 16)
                    sp.dma_start(sh2[:, s, :], K.rows[layer, s, V_SH2].partition_broadcast(P)).then_inc(mod_in, 16)
                sp.dma_start(kT[:], W.peer_keys[layer]).then_inc(small_in, 16)
                src = W.peer_wq[layer].rearrange("(k p) n -> p k n", p=P)
                for n in range(4):
                    if n >= 2:
                        sp.wait_ge(q_ready, 4 * (n - 1))
                    sp.dma_start(wq[:, n % 2], src[:, :, n * BANK:(n + 1) * BANK]).then_inc(wq_in[n % 2], 16)

            @block.gpsimd
            def _(pool):
                pool.memset(eps[:], EPS).then_inc(eps_ready, 1)

            @block.scalar
            def _(act):
                own = Own(act, a_own)
                act.wait_ge(eps_ready, 1)
                for t in OT:
                    own.then(act.activation(junk[:], K.x[:, t, :], ACT.Square, accum_out=ss[:, 0, t:t + 1]))
                own.then(act.activation(ss[:, 1, t0:], ss[:, 0, t0:], ACT.Ln, bias=eps[:], scale=1.0 / D))
                act.activation(ss[:, 2, t0:], ss[:, 1, t0:], ACT.Exp, scale=-0.5).then_inc(rstd_ready, 1)
                act.wait_ge(h2T_ready, NT)
                for k in range(KD):
                    act.activation(h2T[:, k, c0:], bank[k][:, c0:], ACT.Copy).then_inc(h2T_out, 1)
                for f in range(16):
                    act.wait_ge(q_ready, f + 1)
                    act.activation(qT[:, f, c0:], bank[f % 4][:, c0:], ACT.Copy).then_inc(q_out, 1)
                for n in range(4 * NT):
                    act.wait_ge(s_ready, n + 1)
                    act.activation(K.sc[:, n * BANK:(n + 1) * BANK], bank[4 + n % 4][:], ACT.Copy).then_inc(s_out, 1)

            @block.vector
            def _(dve):
                own = Own(dve, v_own)
                dve.wait_ge(rstd_ready, 1)
                dve.wait_ge(mod_in, 64)
                for n, t in enumerate(OT):
                    own.then(dve.scalar_tensor_tensor(out=K.h2[:, t, :], in0=K.x[:, t, :], scalar=ss[:, 2, t:t + 1],
                                                      in1=a2[:, t // 2, :], op0=ALU.mult, op1=ALU.mult))
                    dve.tensor_tensor(K.h2[:, t, :], K.h2[:, t, :], sh2[:, t // 2, :], ALU.add).then_inc(h2_ready, 1)

            @block.tensor
            def _(pe):
                ident = K.cst[:, C_ID:C_ID + P]
                for n, t in enumerate(OT):
                    pe.wait_ge(h2_ready, n + 1)
                    for k in range(KD):
                        mm = pe.transpose(bank[k][:, t * P:(t + 1) * P], K.h2[:, t, k * P:(k + 1) * P], ident)
                    mm.then_inc(h2T_ready, 1)
                pe.wait_ge(h2T_out, KD)
                for f in range(16):
                    if f % 4 == 0:
                        pe.wait_ge(wq_in[f // 4 % 2], 16 * (f // 8 + 1))
                    if f >= 4:
                        pe.wait_ge(q_out, f - 3)
                    for k in range(KD):
                        mm = pe.matmul(bank[f % 4][:, c0:], wq[:, f // 4 % 2, k, (f % 4) * P:(f % 4 + 1) * P], h2T[:, k, c0:],
                                       start=(k == 0), stop=(k == KD - 1))
                    mm.then_inc(q_ready, 1)
                pe.wait_ge(q_out, 16)
                pe.wait_ge(small_in, 16)
                for n in range(4 * NT):
                    t = OT[n // 4]
                    if n >= 4:
                        pe.wait_ge(s_out, n - 3)
                    for j in range(4):
                        f = 4 * (n % 4) + j
                        mm = pe.matmul(bank[4 + n % 4][:, j * P:(j + 1) * P], qT[:, f, t * P:(t + 1) * P], kT[:, f, :],
                                       start=True, stop=True)
                    mm.then_inc(s_ready, 1)


def expert_phase(nc, K, W, layer):
    with ExitStack() as ctx:
        ph = Phase(nc, ctx, f"exp{layer}")
        t0 = 0 if layer == 0 else 2
        G = (TILES - t0) * PAIRS
        LEAD = 2
        U = ph.sb("U", [P, UR, D])
        V = ph.sb("V", [P, VR, D])
        dg = ph.sb("dg", [P, DR, P])
        hc = ph.sb("hc", [P, D])
        st = ph.sb("st", [P, 4, P])
        s2 = ph.sb("s2", [P, 4, P])
        tv = ph.sb("tv", [P, 4, TOPK])
        ti = ph.sb("ti", [P, 4, TOPK], U32)
        tf = ph.sb("tf", [P, 4, TOPK])
        cs = ph.sb("cs", [P, 2, NC])
        ce = ph.sb("ce", [P, 2, NC])
        cs2 = ph.sb("cs2", [P, 2, NC])
        bv = ph.sb("bv", [P, 2, TOPK])
        be = ph.sb("be", [P, 2, TOPK])
        bi = ph.sb("bi", [P, 2, TOPK], U32)
        bf = ph.sb("bf", [P, 2, TOPK])
        eq = ph.sb("eq", [P, 2, TOPK, NC])
        ef = ph.sb("ef", [P, PAIR])
        sm = ph.sb("sm", [P, 2, 2])
        ids = ph.sb("ids", [P, G * PAIR], U32)
        gate = ph.sb("gate", [P, G * PAIR])
        idu = ph.sb("idu", [P, 2, PAIR], U32)
        idv = ph.sb("idv", [P, 2, PAIR], U32)
        a = ph.sb("a", [P, PAIR])
        ga = ph.sb("ga", [P, PAIR])
        wt = ph.sb("wt", [P, PAIR])
        yt = ph.sb("yt", [P, D])
        gt2 = ph.sb("gt2", [P, 2 * D])
        gt2_in = ph.sem("gt2_in")
        u_in = [ph.sem(f"u_in{i}") for i in range(UR)]
        v_in = [ph.sem(f"v_in{i}") for i in range(VR)]
        u_used, v_used = ph.sem("u_used"), ph.sem("v_used")
        ids_ready, idu_ready, idv_ready = ph.sem("ids_ready"), ph.sem("idu_ready"), ph.sem("idv_ready")
        best_ready, soft_ready = ph.sem("best_ready"), ph.sem("soft_ready")
        a_ready, gelu_ready, wt_ready = ph.sem("a_ready"), ph.sem("gelu_ready"), ph.sem("wt_ready")
        dg_ready = ph.sem("dg_ready")
        acc_free = ph.sem("acc_free")
        pace = ph.sem("pace")
        v_own = ph.sem("v_own")
        acc = [K.bank[0], K.bank[1]]
        u_tab = W.peer_u.rearrange("l e d -> (l e) d")
        v_tab = W.peer_v.rearrange("l e d -> (l e) d")
        with nc.Block() as block:
            @block.sync
            def _(sp):
                for s in range(2):
                    sp.dma_start(gt2[:, s * D:(s + 1) * D], K.rows[layer, s, V_GT2].partition_broadcast(P)).then_inc(gt2_in, 16)

            @block.gpsimd
            def _(pool):

                def body(g, par, u, v):
                    if u:
                        pool.wait_ge(ids_ready, g + 1)
                        pool.sem_inc(pace, 1)
                        if not (isinstance(g, int) and g < 2):
                            pool.wait_ge(u_used, PAIR * (g - 1) + UR)
                            pool.sem_inc(pace, 1)
                        pool.tensor_copy(idu[:, par], ids[:, bass.ds(g * PAIR, PAIR)]).then_inc(idu_ready, 1)
                    if v:
                        if not (isinstance(g, int) and g < 2):
                            pool.wait_ge(v_used, PAIR * (g - 2) + VR)
                            pool.sem_inc(pace, 1)
                        pool.tensor_copy(idv[:, 1 - par], ids[:, bass.ds((g - 1) * PAIR, PAIR)]).then_inc(idv_ready, 1)
                    for k in range(PAIR):
                        if u:
                            if k == 0:
                                pool.wait_ge(idu_ready, g + 1)
                                pool.sem_inc(pace, 1)
                            pool.wait_ge(u_used, PAIR * g + k + 1)
                            pool.sem_inc(pace, 1)
                            pool.indirect_dma_start(out=U[:, k % UR, :], out_offset=None, in_=u_tab,
                                                    in_offset=bass.IndirectOffsetOnAxis(ap=idu[:, par, k:k + 1], axis=0)).then_inc(u_in[k % UR], 16)
                        if v:
                            if k == 0:
                                pool.wait_ge(idv_ready, g)
                                pool.sem_inc(pace, 1)
                            pool.wait_ge(v_used, PAIR * (g - 1) + k + 1)
                            pool.sem_inc(pace, 1)
                            pool.indirect_dma_start(out=V[:, k % VR, :], out_offset=None, in_=v_tab,
                                                    in_offset=bass.IndirectOffsetOnAxis(ap=idv[:, 1 - par, k:k + 1], axis=0)).then_inc(v_in[k % VR], 16)

                body(0, 0, True, False)
                body(1, 1, True, True)
                with pool.Fori(2, G - 1, 2) as g:
                    body(g, 0, True, True)
                    body(g + 1, 1, True, True)
                body(G, 0, False, True)

            @block.vector
            def _(dve):
                own = Own(dve, v_own)

                t4 = tf[:].rearrange("p (h q) k -> p h q k", q=2)
                v4 = tv[:].rearrange("p (h q) k -> p h q k", q=2)

                def pick_halves(g):
                    own.then(dve.tensor_copy(st[:].rearrange("p l k -> p (l k)"), K.sc[:, bass.ds(g * BANK, BANK)]))
                    for l in range(4):
                        own(dve.max(tv[:, l, 0:8], st[:, l]))
                    own.wait()
                    for l in range(4):
                        own(dve.max_index(ti[:, l, 0:8], tv[:, l, 0:8], st[:, l]))
                        own(dve.match_replace(s2[:, l], tv[:, l, 0:8], st[:, l], FILL))
                    own.wait()

                def pick_rest(g):
                    for l in range(4):
                        own(dve.max(tv[:, l, 8:16], s2[:, l]))
                    own.wait()
                    for l in range(4):
                        own(dve.max_index(ti[:, l, 8:16], tv[:, l, 8:16], s2[:, l]))
                    own.wait()
                    own.then(dve.tensor_copy(tf[:], ti[:]))
                    own.then(dve.tensor_scalar(t4[:, :, 0, :], t4[:, :, 0, :], float(P), None, ALU.mult))

                def pick_sums(g):
                    off = 0
                    for i in range(8):
                        n = ROWN[i]
                        for dst, src in ((cs, v4), (ce, t4)):
                            own(dve.tensor_tensor(dst[:, :, off:off + n], src[:, :, 0, i:i + 1].broadcast_to([P, 2, n]),
                                                  src[:, :, 1, 0:n], ALU.add))
                        off += n
                    for dst, src in ((cs, v4), (ce, t4)):
                        own(dve.tensor_tensor(dst[:, :, off:NC], src[:, :, 0, 8:16], src[:, :, 1, 0:1].broadcast_to([P, 2, 8]), ALU.add))
                    own.wait()
                    for h in range(2):
                        own(dve.max(bv[:, h, 0:8], cs[:, h]))
                    own.wait()
                    for h in range(2):
                        own(dve.max_index(bi[:, h, 0:8], bv[:, h, 0:8], cs[:, h]))
                        own(dve.match_replace(cs2[:, h], bv[:, h, 0:8], cs[:, h], FILL))
                    own.wait()
                    for h in range(2):
                        own(dve.max(bv[:, h, 8:16], cs2[:, h]))
                    own.wait()
                    for h in range(2):
                        own(dve.max_index(bi[:, h, 8:16], bv[:, h, 8:16], cs2[:, h]))
                    own.then(dve.tensor_tensor(be[:], bv[:], bv[:, :, 0:1].broadcast_to([P, 2, TOPK]), ALU.subtract))
                    dve.sem_inc(best_ready, 1)

                def pick_number(g):
                    own.then(dve.tensor_copy(bf[:], bi[:]))
                    own.then(dve.tensor_tensor(eq[:], K.cst[:, C_IOTA:C_END].unsqueeze(1).unsqueeze(1).broadcast_to([P, 2, TOPK, NC]),
                                               bf[:].unsqueeze(3).broadcast_to([P, 2, TOPK, NC]), ALU.is_equal))
                    own.then(dve.tensor_tensor(eq[:], eq[:], ce[:].unsqueeze(2).broadcast_to([P, 2, TOPK, NC]), ALU.mult))
                    own.then(dve.tensor_reduce(ef[:].rearrange("p (h k) -> p h k", h=2), eq[:], AX.X, ALU.add))
                    own.then(dve.tensor_scalar(ids[:, bass.ds(g * PAIR, PAIR)], ef[:], float(layer * NEXP), None, ALU.add))
                    dve.sem_inc(ids_ready, 1)

                def pick_gate(g):
                    dve.wait_ge(soft_ready, g + 1)
                    own(dve.tensor_reduce(sm[:, 0, :], be[:], AX.X, ALU.add))
                    own.wait()
                    own.then(dve.reciprocal(sm[:, 1, :], sm[:, 0, :]))
                    own.then(dve.tensor_tensor(gate[:, bass.ds(g * PAIR, PAIR)].rearrange("p (h k) -> p h k", h=2), be[:],
                                               sm[:, 1, :].unsqueeze(2).broadcast_to([P, 2, TOPK]), ALU.mult))

                def pick(g, part=None):
                    for n, stage in enumerate((pick_halves, pick_rest, pick_sums, pick_number, pick_gate)):
                        if part in (None, n):
                            stage(g)

                def collect(g):
                    tile = g // PAIRS + t0
                    dve.wait_ge(v_used, PAIR * (g + 1) + VR)
                    for half in range(2):
                        own(dve.tensor_tensor(yt[:, half * BANK:(half + 1) * BANK], acc[half][:],
                                              gt2[:, bass.ds((tile // 2) * D + half * BANK, BANK)], ALU.mult))
                    own.wait()
                    dve.sem_inc(acc_free, 1)
                    xs = K.xf[:, bass.ds(tile * D, D)]
                    own.then(dve.tensor_tensor(xs, xs, yt[:], ALU.add))

                def body(g, picks, collects):
                    own.then(dve.tensor_copy(hc[:], K.h2f[:, bass.ds((g // PAIRS + t0) * D, D)]))
                    for k in range(PAIR):
                        dve.wait_ge(u_in[k % UR], 16 * ((PAIR // UR) * g + k // UR + 1))
                        dve.tensor_tensor_reduce(U[:, k % UR, :], U[:, k % UR, :], hc[:], 1.0, 0.0, ALU.mult, ALU.add,
                                                 a[:, k:k + 1]).then_inc(u_used, 1)
                        if k == 4 and isinstance(g, int) and g == 0:
                            pick(1)
                        if k % 6 == 5 and picks:
                            pick(g + LEAD, k // 6)
                    dve.wait_ge(u_used, PAIR * (g + 1) + UR)
                    dve.sem_inc(a_ready, 1)
                    if collects:
                        collect(g - 1)
                    dve.wait_ge(gelu_ready, g + 1)
                    dve.tensor_tensor(wt[:], ga[:], gate[:, bass.ds(g * PAIR, PAIR)], ALU.mult).then_inc(wt_ready, 1)
                    own.clear()

                dve.sem_inc(u_used, UR)
                dve.wait_ge(gt2_in, 32)
                pick(0)
                own.clear()
                body(0, True, False)
                with dve.Fori(1, G - LEAD) as g:
                    body(g, True, True)
                for g in range(G - LEAD, G):
                    body(g, False, True)
                collect(G - 1)

            @block.scalar
            def _(act):
                def soft(g):
                    act.wait_ge(best_ready, g + 1)
                    act.activation(be[:], be[:], ACT.Exp).then_inc(soft_ready, 1)

                def body(g, picks):
                    if picks:
                        soft(g + LEAD)
                    act.wait_ge(a_ready, g + 1)
                    act.activation(ga[:], a[:], ACT.Gelu).then_inc(gelu_ready, 1)

                def diags(g, picks=False):
                    act.wait_ge(wt_ready, g + 1)
                    for k in range(PAIR):
                        act.wait_ge(v_used, PAIR * g + k + 1)
                        act.activation(dg[:, k % DR, :], K.cst[:, C_ID:C_ID + P], ACT.Copy, scale=wt[:, k:k + 1]).then_inc(dg_ready, 1)
                        if picks and k == 20:
                            soft(g + 1 + LEAD)

                soft(0)
                soft(1)
                body(0, True)
                with act.Fori(1, G - LEAD) as g:
                    diags(g - 1, True)
                    body(g, False)
                for g in range(G - LEAD, G):
                    diags(g - 1)
                    body(g, False)
                diags(G - 1)

            @block.tensor
            def _(pe):
                def body(g):
                    pe.wait_ge(acc_free, g + 1)
                    for k in range(PAIR):
                        pe.wait_ge(dg_ready, PAIR * g + k + 1)
                        pe.wait_ge(v_in[k % VR], 16 * ((PAIR // VR) * g + k // VR + 1))
                        for half in range(2):
                            mm = pe.matmul(acc[half][:], dg[:, k % DR, :], V[:, k % VR, half * BANK:(half + 1) * BANK],
                                           start=(k == 0), stop=(k == PAIR - 1))
                        mm.then_inc(v_used, 1)

                pe.sem_inc(v_used, VR)
                pe.sem_inc(acc_free, 1)
                with pe.Fori(0, G) as g:
                    body(g)


def final_phase(nc, K, W, out):
    with ExitStack() as ctx:
        ph = Phase(nc, ctx, "fin")
        w = ph.sb("w", [P, D])
        y = ph.sb("y", [P, 2, D])
        junk = ph.sb("junk", [P, D])
        ss = ph.sb("ss", [P, 3, 2])
        eps = ph.sb("eps", [P, 1])
        w_in, eps_ready, rstd_ready, y_ready, y_out, a_own = (ph.sem(n) for n in ("w_in", "eps_ready", "rstd_ready", "y_ready", "y_out", "a_own"))
        with nc.Block() as block:
            @block.sync
            def _(sp):
                sp.dma_start(w[:], W.final_norm.partition_broadcast(P)).then_inc(w_in, 16)
                for t in range(2):
                    sp.wait_ge(y_ready, t + 1)
                    sp.dma_start(out[0, t * P:(t + 1) * P, :], y[:, t, :]).then_inc(y_out, 16)
                sp.wait_ge(y_out, 32)

            @block.gpsimd
            def _(pool):
                pool.memset(eps[:], EPS).then_inc(eps_ready, 1)

            @block.scalar
            def _(act):
                own = Own(act, a_own)
                act.wait_ge(eps_ready, 1)
                for t in range(2):
                    own.then(act.activation(junk[:], K.x[:, 2 + t, :], ACT.Square, accum_out=ss[:, 0, t:t + 1]))
                own.then(act.activation(ss[:, 1, :], ss[:, 0, :], ACT.Ln, bias=eps[:], scale=1.0 / D))
                act.activation(ss[:, 2, :], ss[:, 1, :], ACT.Exp, scale=-0.5).then_inc(rstd_ready, 1)

            @block.vector
            def _(dve):
                dve.wait_ge(w_in, 16)
                dve.wait_ge(rstd_ready, 1)
                for t in range(2):
                    dve.scalar_tensor_tensor(out=y[:, t, :], in0=K.x[:, 2 + t, :], scalar=ss[:, 2, t:t + 1], in1=w[:],
                                             op0=ALU.mult, op1=ALU.mult).then_inc(y_ready, 1)


def program(nc, W, out, stop=None, dump=None):
    with ExitStack() as ctx:
        K = Keep()

        def sb(name, shape, dt=F32):
            return ctx.enter_context(nc.sbuf_tensor(name, shape, dt))

        K.bank = [ctx.enter_context(nc.psum_tensor(f"bank{i}", [P, BANK], F32)) for i in range(8)]
        K.cst = sb("cst", [P, C_END])
        K.x = sb("x_res", [P, TILES, D])
        K.xf = K.x[:].rearrange("p t d -> p (t d)")
        K.rows = nc.dram_tensor("mod_rows", [DEPTH, 2, 4, D], F32).ap()
        K.modT = sb("modT", [P, 2, KD, 2])
        for layer in range(DEPTH):
            mod_phase(nc, K, W, layer)
            with ExitStack() as mid:
                def sm(name, shape, dt=F32):
                    return mid.enter_context(nc.sbuf_tensor(f"{name}{layer}", shape, dt))
                K.hT = sm("hT", [P, KD, TOK])
                K.pT = sm("pT", [P, 4, TOK])
                K.zT = sm("zT", [P, 4, TOK])
                K.ba = sm("ba", [P, TILES, 16])
                with ExitStack() as q:
                    K.qkv = q.enter_context(nc.sbuf_tensor(f"qkv{layer}", [P, 12, TOK], F32))
                    inproj_phase(nc, K, W, layer)
                    delta_phase(nc, K, W, layer)
                merge_phase(nc, K, W, layer)
            with ExitStack() as mid:
                K.h2 = mid.enter_context(nc.sbuf_tensor(f"h2_{layer}", [P, TILES, D], F32))
                K.h2f = K.h2[:].rearrange("p t d -> p (t d)")
                K.sc = mid.enter_context(nc.sbuf_tensor(f"sc{layer}", [P, TILES * 2048], F32))
                query_phase(nc, K, W, layer)
                expert_phase(nc, K, W, layer)
        final_phase(nc, K, W, out)


class _Dram:
    pass


_INS = ['x', 'c', 'ctx', 'c_ctx', 'w_mod', 'b_mod', 'norm_mix', 'w_in', 'conv_w', 'a_log', 'dt_bias', 'dn_out_norm',
        'pool_w', 'pool_scale', 'w_up_dn', 'w_up_pool', 'w_out', 'norm_ffn', 'peer_wq', 'peer_keys', 'peer_u', 'peer_v',
        'final_norm']


def kernel(**inputs):
    import concourse.bacc as _bacc
    from concourse.bass_utils import run_bass_kernel_spmd as _run

    nc = _bacc.Bacc("TRN2", target_bir_lowering=False, num_devices=1)
    arrays, W = {}, _Dram()
    cst, levels, icnt = constants()
    named = {n: np.ascontiguousarray(inputs[n]) for n in _INS}
    named["conv_w"] = np.ascontiguousarray(named["conv_w"].reshape(DEPTH, CONV, 12, P).transpose(0, 3, 1, 2))
    named["pool_scale"] = np.ascontiguousarray(named["pool_scale"].reshape(DEPTH, 4, P).transpose(0, 2, 1))
    named["peer_keys"] = np.ascontiguousarray(named["peer_keys"].reshape(DEPTH, 16, P, P).transpose(0, 3, 1, 2))
    for name, a in {**named, "cst": cst, "levels": levels, "icnt": icnt}.items():
        arrays[f"in_{name}"] = a
        W.__dict__[name] = nc.dram_tensor(f"in_{name}", a.shape, mybir.dt.from_np(a.dtype), kind="ExternalInput").ap()
    out = nc.dram_tensor("out", (1, SEQ, D), F32, kind="ExternalOutput").ap()
    program(nc, W, out)
    r = _run(nc, [arrays], core_ids=[0])
    return r.results[0]["out"]
```
